# Optimizing a Trainium2 kernel written in Bass

```python
import jax, jax.numpy as jnp
from jax import lax
import numpy as np

D_MODEL = 1024
BATCH = 1
SEQ = 256
DEPTH = 1
DEC_BATCH = 8
DEC_SEQ = 1
PAST_LEN = 2048
PAGE_SIZE = 128

MIX_WIDTH = D_MODEL
HG_HEADS = 4
HG_DV = (MIX_WIDTH // 2) // HG_HEADS
HG_DK = HG_DV
GLA_HEADS = 4
GLA_DV = (MIX_WIDTH // 2) // GLA_HEADS
GLA_DK = GLA_DV // 2
GLA_GATE_RANK = 16
GLA_GATE_NORM = 16.0
CHUNK = 64
N_EXPERTS = 32
TOP_K = 4
D_FF = D_MODEL
SWIGLU_LIMIT = 7.0
SWIGLU_ALPHA = 1.702
MOE_BLOCK = 128
EPS = 1e-6
PROJ_WIDTHS = (HG_HEADS * HG_DK, HG_HEADS * HG_DK, HG_HEADS * HG_DV, HG_HEADS * HG_DV,
               GLA_HEADS * GLA_DK, GLA_HEADS * GLA_DK, GLA_HEADS * GLA_DV, GLA_HEADS * GLA_DV,
               GLA_GATE_RANK)
D_IN_PROJ = sum(PROJ_WIDTHS)

kernel_name = "hymba_hgrn2_gla_moe_adaln_step"

def rms_norm(x, g):
    xf = x.astype(jnp.float32)
    y = xf * lax.rsqrt(jnp.mean(xf * xf, axis=-1, keepdims=True) + EPS)
    return (y * g.astype(jnp.float32)).astype(x.dtype)

def gated_recurrence(q, k, v, log_a, s0):
    B, L, H, DK = q.shape
    DV = v.shape[-1]
    C = min(CHUNK, L)
    n = -(-L // C)
    pad = n * C - L
    if pad:
        pw = ((0, 0), (0, pad), (0, 0), (0, 0))
        q, k, v, log_a = (jnp.pad(t, pw) for t in (q, k, v, log_a))

    def to_chunks(t):
        return t.reshape(B, n, C, H, t.shape[-1]).transpose(1, 0, 3, 2, 4)

    causal = jnp.tril(jnp.ones((C, C), dtype=bool))[:, :, None]

    def step(S, inp):
        qc, kc, vc, gc = inp
        b = jnp.cumsum(gc, axis=2)
        diff = b[:, :, :, None, :] - b[:, :, None, :, :]
        decay = jnp.exp(jnp.where(causal, diff, -jnp.inf))
        att = jnp.einsum('bhtd,bhsd,bhtsd->bhts', qc, kc, decay)
        o = jnp.einsum('bhts,bhsv->bhtv', att, vc) + jnp.einsum('bhtd,bhdv->bhtv', qc * jnp.exp(b), S)
        b_last = b[:, :, -1:, :]
        S_new = jnp.exp(b_last[:, :, 0, :])[..., None] * S + jnp.einsum(
            'bhsd,bhsv->bhdv', kc * jnp.exp(b_last - b), vc)
        return S_new, o

    S, o = lax.scan(step, s0, (to_chunks(q), to_chunks(k), to_chunks(v), to_chunks(log_a)))
    o = o.transpose(1, 0, 3, 2, 4).reshape(B, n * C, H, DV)[:, :L]
    return o, S

def token_mixers(h, s_hg, s_gl, lb, w_in, w_gk2, b_gk2, gn_hg, gn_gl, w_o):
    B, L, _ = h.shape
    f32 = jnp.float32
    proj = h @ w_in
    splits = np.cumsum(PROJ_WIDTHS)[:-1].tolist()
    hq, hf, hi, hg, gq, gk, gv, gg, gr = jnp.split(proj, splits, axis=-1)

    def heads(t, nh):
        return t.reshape(B, L, nh, -1).astype(f32)

    z = heads(hf, HG_HEADS)
    lb_h = lb.reshape(HG_HEADS, HG_DK).astype(f32)
    log_f = jnp.logaddexp(jnp.log(lb_h), jnp.log1p(-lb_h) + jax.nn.log_sigmoid(z))
    k_h = (1.0 - lb_h) * jax.nn.sigmoid(-z)
    q_h = jax.nn.silu(heads(hq, HG_HEADS))
    o_h, s_hg_new = gated_recurrence(q_h, k_h, heads(hi, HG_HEADS), log_f, s_hg.astype(f32))
    o_h = rms_norm(o_h, gn_hg) * jax.nn.silu(heads(hg, HG_HEADS))

    q_g = heads(gq, GLA_HEADS) * (GLA_DK ** -0.5)
    k_g = heads(gk, GLA_HEADS)
    v_g = heads(gv, GLA_HEADS)
    log_a = jax.nn.log_sigmoid((gr @ w_gk2 + b_gk2).astype(f32)).reshape(B, L, GLA_HEADS, GLA_DK) / GLA_GATE_NORM
    o_g, s_gl_new = gated_recurrence(q_g, k_g, v_g, log_a, s_gl.astype(f32))
    o_g = rms_norm(o_g, gn_gl) * jax.nn.silu(heads(gg, GLA_HEADS))

    o = jnp.concatenate([o_h.reshape(B, L, -1), o_g.reshape(B, L, -1)], axis=-1).astype(h.dtype)
    return o @ w_o, s_hg_new, s_gl_new

def moe_ffn(h, router_w, router_b, w_up, b_up, w_down, b_down):
    B, L, D = h.shape
    T = B * L
    x2d = h.reshape(T, D)
    logits = (x2d @ router_w + router_b).astype(jnp.float32)
    top_val, top_idx = lax.top_k(logits, TOP_K)
    gate = jax.nn.softmax(top_val, axis=-1)
    M = T * TOP_K
    flat_e = top_idx.reshape(M)
    order = jnp.argsort(flat_e)
    sorted_e = flat_e[order]
    sorted_tok = order // TOP_K
    sorted_gate = gate.reshape(M)[order]
    counts = jnp.bincount(flat_e, length=N_EXPERTS)
    padded = (counts + MOE_BLOCK - 1) // MOE_BLOCK * MOE_BLOCK
    start = jnp.cumsum(counts) - counts
    padded_end = jnp.cumsum(padded)
    padded_start = padded_end - padded
    dest = padded_start[sorted_e] + jnp.arange(M) - start[sorted_e]
    n_blocks = -(-M // MOE_BLOCK) + N_EXPERTS
    rows = n_blocks * MOE_BLOCK
    row_tok = jnp.zeros((rows,), jnp.int32).at[dest].set(sorted_tok)
    block_e = jnp.minimum(jnp.searchsorted(padded_end, jnp.arange(n_blocks) * MOE_BLOCK, side='right'),
                          N_EXPERTS - 1)
    xb = x2d[row_tok].reshape(n_blocks, MOE_BLOCK, D)

    def expert_block(args):
        xblk, e = args
        u = xblk @ w_up[e] + b_up[e]
        glu, lin = jnp.split(u, 2, axis=-1)
        glu = jnp.minimum(glu, SWIGLU_LIMIT)
        lin = jnp.clip(lin, -SWIGLU_LIMIT, SWIGLU_LIMIT)
        act = glu * jax.nn.sigmoid(SWIGLU_ALPHA * glu) * (lin + 1.0)
        return act @ w_down[e] + b_down[e]

    yb = lax.map(expert_block, (xb, block_e)).reshape(rows, D)
    y = jax.ops.segment_sum(yb[dest] * sorted_gate[:, None].astype(yb.dtype), sorted_tok, num_segments=T)
    return y.reshape(B, L, D)

def decoder_layer(x, c, s_hg, s_gl, lb, norm1_g, norm2_g, w_ada, b_ada, w_in, w_gk2, b_gk2,
                  gn_hg, gn_gl, w_o, router_w, router_b, w_up, b_up, w_down, b_down):
    mod = (jax.nn.silu(c) @ w_ada + b_ada)[:, None, :]
    sh1, sc1, g1, sh2, sc2, g2 = jnp.split(mod, 6, axis=-1)
    h = rms_norm(x, norm1_g) * (1.0 + sc1) + sh1
    o, s_hg_new, s_gl_new = token_mixers(h, s_hg, s_gl, lb, w_in, w_gk2, b_gk2, gn_hg, gn_gl, w_o)
    x = x + g1 * o
    h = rms_norm(x, norm2_g) * (1.0 + sc2) + sh2
    x = x + g2 * moe_ffn(h, router_w, router_b, w_up, b_up, w_down, b_down)
    return x, s_hg_new, s_gl_new

def setup_inputs(seed: int = 0) -> dict:
    key = jax.random.key(seed)
    ks = jax.random.split(key, 26)
    D = D_MODEL

    def nrm(k, shape, s):
        return jax.random.normal(k, shape, jnp.float32) * s

    return {
        "x_prompt": nrm(ks[0], (BATCH, SEQ, D), 1.0),
        "x_sample": nrm(ks[1], (DEC_BATCH, DEC_SEQ, D), 1.0),
        "state_hgrn": nrm(ks[2], (DEPTH, DEC_BATCH, HG_HEADS, HG_DK, HG_DV), 0.3),
        "state_gla": nrm(ks[3], (DEPTH, DEC_BATCH, GLA_HEADS, GLA_DK, GLA_DV), 0.3),
        "c_prompt": nrm(ks[4], (BATCH, D), 1.0),
        "c_sample": nrm(ks[5], (DEC_BATCH, D), 1.0),
        "hgrn_lower_bounds": nrm(ks[6], (DEPTH, HG_HEADS * HG_DK), 1.0),
        "norm1_g": 1.0 + nrm(ks[7], (DEPTH, D), 0.02),
        "norm2_g": 1.0 + nrm(ks[8], (DEPTH, D), 0.02),
        "w_ada": nrm(ks[9], (DEPTH, D, 6 * D), 0.3 * D ** -0.5),
        "b_ada": nrm(ks[10], (DEPTH, 6 * D), 0.02),
        "w_in": nrm(ks[11], (DEPTH, D, D_IN_PROJ), D ** -0.5),
        "w_gk2": nrm(ks[12], (DEPTH, GLA_GATE_RANK, GLA_HEADS * GLA_DK), GLA_GATE_RANK ** -0.5),
        "b_gk2": nrm(ks[13], (DEPTH, GLA_HEADS * GLA_DK), 0.1),
        "gn_hgrn": 1.0 + nrm(ks[14], (DEPTH, HG_DV), 0.02),
        "gn_gla": 1.0 + nrm(ks[15], (DEPTH, GLA_DV), 0.02),
        "w_o": nrm(ks[16], (DEPTH, MIX_WIDTH, D), MIX_WIDTH ** -0.5),
        "router_w": nrm(ks[17], (DEPTH, D, N_EXPERTS), D ** -0.5),
        "router_b": nrm(ks[18], (DEPTH, N_EXPERTS), 0.01),
        "w_up": nrm(ks[19], (DEPTH, N_EXPERTS, D, 2 * D_FF), D ** -0.5),
        "b_up": nrm(ks[20], (DEPTH, N_EXPERTS, 2 * D_FF), 0.01),
        "w_down": nrm(ks[21], (DEPTH, N_EXPERTS, D_FF, D), D_FF ** -0.5),
        "b_down": nrm(ks[22], (DEPTH, N_EXPERTS, D), 0.01),
        "final_norm_g": 1.0 + nrm(ks[23], (D,), 0.02),
    }

def reference(x_prompt, x_sample, state_hgrn, state_gla, c_prompt, c_sample, hgrn_lower_bounds,
              norm1_g, norm2_g, w_ada, b_ada, w_in, w_gk2, b_gk2, gn_hgrn, gn_gla, w_o,
              router_w, router_b, w_up, b_up, w_down, b_down, final_norm_g):
    f32 = jnp.float32
    lbs = jnp.cumsum(jax.nn.softmax(hgrn_lower_bounds.astype(f32), axis=0), axis=0)
    lbs = lbs - lbs[0:1]
    B = x_prompt.shape[0]
    yp, ys = x_prompt, x_sample
    hg_p, gl_p, hg_s, gl_s = [], [], [], []
    for l in range(DEPTH):
        layer_w = (lbs[l], norm1_g[l], norm2_g[l], w_ada[l], b_ada[l], w_in[l], w_gk2[l], b_gk2[l],
                   gn_hgrn[l], gn_gla[l], w_o[l], router_w[l], router_b[l], w_up[l], b_up[l],
                   w_down[l], b_down[l])
        zero_hg = jnp.zeros((B, HG_HEADS, HG_DK, HG_DV), f32)
        zero_gl = jnp.zeros((B, GLA_HEADS, GLA_DK, GLA_DV), f32)
        yp, shp, sgp = decoder_layer(yp, c_prompt, zero_hg, zero_gl, *layer_w)
        ys, shs, sgs = decoder_layer(ys, c_sample, state_hgrn[l], state_gla[l], *layer_w)
        hg_p.append(shp.astype(x_prompt.dtype))
        gl_p.append(sgp.astype(x_prompt.dtype))
        hg_s.append(shs.astype(state_hgrn.dtype))
        gl_s.append(sgs.astype(state_gla.dtype))
    y_prompt = rms_norm(yp, final_norm_g)
    y_sample = rms_norm(ys, final_norm_g)
    new_hgrn_prompt = jnp.stack(hg_p)
    new_gla_prompt = jnp.stack(gl_p)
    new_hgrn_sample = jnp.stack(hg_s)
    new_gla_sample = jnp.stack(gl_s)
    return (y_prompt, y_sample, new_hgrn_prompt, new_gla_prompt, new_hgrn_sample, new_gla_sample)


_drawn_inputs = setup_inputs


def setup_inputs(seed=0):
    import zlib

    import numpy as np

    out = dict(_drawn_inputs(seed))
    spreads = {}
    factors = {'norm2_g': 4.928,
     'gn_hgrn': 21.618,
     'gn_gla': 8.0,
     'router_b': 8.0,
     'b_up': 23.854,
     'b_down': 64.0,
     'final_norm_g': 8.423}
    for name, (base, spread) in spreads.items():
        noise = np.random.default_rng([zlib.crc32(name.encode()), seed]).standard_normal(out[name].shape)
        drawn = base * np.exp(spread * noise) if base else spread * noise
        out[name] = __import__('jax').numpy.asarray(drawn.astype(out[name].dtype))
    for name, factor in factors.items():
        out[name] = (out[name] * factor).astype(out[name].dtype)
    return out
```

```python
from contextlib import ExitStack

import concourse.bass as bass
from concourse import mybir

F = mybir.dt.float32
I32 = mybir.dt.int32
U32 = mybir.dt.uint32
U8 = mybir.dt.uint8
ALU = mybir.AluOpType
ACT = mybir.ActivationFunctionType
AX = mybir.AxisListType

P = 128
D = 1024
KT = D // P
TP = 256
TS = 8
T = TP + TS
NC = TP // P
NE = 32
TOPK = 4
BLK = 64
EXTRA = 16
LEVELS = [1, 2, 4, 8, 16, 32, 64]
EPS = 1e-6
ALPHA = 1.702
LIMIT = 7.0
NQ = 6
NH = 8

SLOTS = 16
ORDER = [0, 1, 2, 3, 8, 9, 10, 11, 12, 13, 14, 15, 4, 5, 6, 7]
PEEL, UNROLL = 3, 4
LOOPS = (NE - 1 - PEEL) // UNROLL
UP_FIRST = 3

FRONT = ([("ada", 0, k) for k in range(8)]
         + [("in", c, s) for c in (1, 0, 2) for s in range(2)]
         + [("ada", 1, k) for k in range(8)] + [("ada", 2, k) for k in range(8)]
         + [("in", c, s) for c in (4, 5, 3, 6) for s in range(2)]
         + [("out", 0, s) for s in range(4)])
NF = len(FRONT)
FRONT_SLOT = [(n - (NF - 8)) % 8 for n in range(NF)]
HF, HQ, HI, HG, GQK, GV, GG = 1, 0, 2, 3, 4, 5, 6
MIDDLE = ([("proj", c, i) for c in (HF, HQ, HI) for i in range(4)]
          + [("ada", 1), ("vt", 0), ("ada", 2)]
          + [("low",), ("lev", 0, 0), ("proj", GQK, 0), ("lev", 0, 1), ("proj", GQK, 1), ("lev", 0, 2),
             ("proj", GQK, 2), ("lev", 0, 3), ("proj", GQK, 3), ("lev", 0, 4), ("y", 0), ("lev", 0, 5),
             ("y", 1), ("lev", 0, 6), ("proj", GV, 0), ("lev", 0, 7)]
          + [("proj", GV, i) for i in range(1, 4)] + [("vt", 1)]
          + [("so", 0), ("proj", HG, 0), ("proj", HG, 1), ("lev", 1, 0), ("kdt",), ("proj", HG, 2), ("lev", 1, 1),
             ("so", 1), ("proj", HG, 3), ("lev", 1, 2), ("proj", GG, 0), ("lev", 1, 3), ("so", 2), ("proj", GG, 1),
             ("lev", 1, 4), ("proj", GG, 2), ("lev", 1, 5), ("proj", GG, 3), ("so", 3),
             ("lev", 1, 6), ("lev", 1, 7), ("state",), ("out",), ("so", 4), ("so", 5)])
PROJ = [t for t in MIDDLE if t[0] in ("proj", "low", "y")]
PROJ_AT = {t: n for n, t in enumerate(PROJ)}
AUX_UNITS = {"vt": 3, "lev": 2, "kdt": 3, "state": 3, "out": 4}
AUX_BANK = [6, 7, 0]
AUX_END = {}
for _task in MIDDLE:
    AUX_END[_task] = max(AUX_END.values(), default=0) + AUX_UNITS.get(_task[0], 0)
FRONT_AT = {what: n for n, what in enumerate(FRONT)}


def front_round(n):
    return sum(FRONT_SLOT[m] == FRONT_SLOT[n] for m in range(n + 1))


FRONT_FILLS = [sum(s == x for x in FRONT_SLOT) for s in range(SLOTS)]


_PLAIN = [not ((kind == "ada" and s == 7) or (kind == "in" and s == 1) or (kind == "out" and s == 3))
          for kind, c, s in FRONT]
FRONT_USED = [sum(_PLAIN[:n + 1]) for n in range(NF)]
FRONT_PLAIN = sum(_PLAIN)


def expert_slot(i):
    return ORDER[i % SLOTS]


class Order:

    def __init__(self, eng, chain):
        self.eng, self.chain, self.count, self.open = eng, chain, {}, {}
        self.keys = {}

    def did(self, ins, sem=None):
        s = self.chain if sem is None else sem
        k = id(s)
        self.keys[k] = s
        self.count[k] = self.count.get(k, 0) + 1
        ins.then_inc(s, 1)
        self.open[k] = self.count[k]
        return ins

    def settle(self):
        for k, v in self.open.items():
            self.eng.wait_ge(self.keys[k], v)
        self.open = {}

    def link(self, ins, sem=None):
        self.did(ins, sem)
        self.settle()

    def at(self, sem, value):
        self.keys[id(sem)] = sem
        self.count[id(sem)] = value


def build_step(nc, a, o):
    ctx = ExitStack()
    with ctx:
        def sb(name, shape, dt=F):
            return ctx.enter_context(nc.sbuf_tensor(name, shape, dt))

        sems = {}

        def sem(name):
            if name not in sems:
                sems[name] = ctx.enter_context(nc.semaphore(name))
            return sems[name]

        ring = sb("ring", [P, SLOTS, 2048])
        bank = ctx.enter_context(nc.psum_tensor("bank", [P, 8, 512], F))

        ident = sb("ident", [P, P])
        ones = sb("ones", [P, P])
        before = sb("before", [P, P])
        iota_slot = sb("iota_slot", [P, BLK])
        iota_exp = sb("iota_exp", [P, NE])
        half_mask = sb("half_mask", [P, 2])
        vecT = sb("vecT", [P, 68])
        modT = sb("modT", [P, 48, 9])
        scale1 = sb("scale1", [P, KT, 9])
        scale2 = sb("scale2", [P, KT, 9])
        bupT = sb("bupT", [P, 16, NE])

        wrt = sb("wrt", [P, KT, NE])
        brt = sb("brt", [P, NE])
        decay_s = sb("decay_s", [P, NQ, TS])
        decay_c = sb("decay_c", [P, NQ])
        rstd = sb("rstd", [P, T])
        qsam = sb("qsam", [P, 2, TS, 2])
        logit = sb("logit", [P, 3, NE])
        top_v = sb("top_v", [P, 3, 8])
        top_i = sb("top_i", [P, 3, 8], U32)
        top_f = sb("top_f", [P, 3, TOPK])
        gate = sb("gate", [P, 3, TOPK])
        gsum = sb("gsum", [P, 3])
        valid = sb("valid", [P, 3])
        picked = sb("picked", [P, 3, NE])
        rank = sb("rank", [P, 3, NE])
        rowid = sb("rowid", [P, 3, NE])
        cnt = sb("cnt", [P, NE])
        nblk = sb("nblk", [P, NE])
        cumb = sb("cumb", [P, NE])
        tmpe = sb("tmpe", [P, NE])
        base1 = sb("base1", [P, NE])
        rowk = sb("rowk", [P, 3, TOPK])
        rowk_i = sb("rowk_i", [P, 3, TOPK], U32)
        iota_blk = sb("iota_blk", [P, EXTRA])
        table_f = sb("table_f", [P, EXTRA + 1])
        table = sb("table", [P, EXTRA + 1], I32)
        ovr = sb("ovr", [P, 3])
        ovbase = sb("ovbase", [P, 1])
        sumsq = sb("sumsq", [P, 4])
        eps_col = sb("eps_col", [P, 1])

        arena = sb("arena", [P, 3 * 2112 + 3168 + 2640 + 2112 + 1024 + 2048])
        at = [0]

        def take(n):
            at[0] += n
            return arena[:, at[0] - n:at[0]]

        r_x, r_tmp, r_h = take(2112), take(2112), take(2112)
        r_qf, r_k, r_gv = take(3168), take(2640), take(2112 + 1024)
        r_s = take(1536 + 512)
        xT = r_x.rearrange("p (k t) -> p k t", k=KT)
        tmpT = r_tmp.rearrange("p (k t) -> p k t", k=KT)
        hT = r_h.rearrange("p (k t) -> p k t", k=KT)
        oT = hT
        qT = r_qf[:, 0:1584].rearrange("p (k t) -> p k t", k=NQ)
        logf = r_qf[:, 1584:3168].rearrange("p (k t) -> p k t", k=NQ)
        kT = r_k[:, 0:1584].rearrange("p (k t) -> p k t", k=NQ)
        kmask = r_k[:, 1584:2640].rearrange("p (k t) -> p k t", k=4)
        vT = r_gv[:, 0:2112].rearrange("p (k t) -> p k t", k=NH)
        gateT = vT
        vbc = r_gv[:, 2112:3136].rearrange("p (b v) -> p b v", b=TS)
        S1 = r_s[:, 0:768].rearrange("p (h v) -> p h v", h=NQ)
        S2 = r_s[:, 768:1536].rearrange("p (h v) -> p h v", h=NQ)
        kd = r_tmp[:, 0:1536].rearrange("p (k t) -> p k t", k=NQ)
        zero = r_s[:, 512:1024]
        wgr = r_s[:, 0:128].rearrange("p (k n) -> p k n", k=KT)
        level_mask = r_s[:, 256:480].bitcast(U8).rearrange("p (m t) -> p m t", m=7)
        grT = r_s[0:16, 1536:1800]
        wgk2 = r_s[0:16, 1024:1280]
        onehot = r_tmp[:, 0:384].rearrange("p (i c e) -> p i c e", i=3, c=TOPK)
        ovw = r_tmp[:, 1536:2048].rearrange("p (j e) -> p j e", j=EXTRA)
        weighted = r_tmp[:, 384:768].rearrange("p (i c e) -> p i c e", i=3, c=TOPK)
        gateE = r_tmp[:, 768:864].rearrange("p (i e) -> p i e", i=3)
        over = r_tmp[:, 864:960].rearrange("p (i e) -> p i e", i=3)
        h2T = r_k[:, 0:2112].rearrange("p (k t) -> p k t", k=KT)
        h2tok = r_qf[:, 0:3072].rearrange("p (i d) -> p i d", i=3)
        x1tok = r_gv[:, 0:3072].rearrange("p (i d) -> p i d", i=3)
        xe = r_h[:, 0:1024].rearrange("p (b k s) -> p b k s", b=2, k=KT)
        us = r_h[:, 1024:2048]
        tg, tl, te, tr = (r_tmp[:, 512 * i:512 * i + 512] for i in range(4))
        ysb = r_x[:, 0:1024].rearrange("p (b n) -> p b n", b=2)
        actT = r_x[:, 1024:1536].rearrange("p (k s) -> p k s", k=KT)
        pick = r_x[:, 1536:1728].rearrange("p (i s) -> p i s", i=3)
        g2row = r_k[:, 0:2048].rearrange("p (i d) -> p i d", i=2)
        fgrow = r_s[:, 0:1024]
        bdn = r_s[0:NE, 1024:2048]
        gateTok = r_x[:, 1728:1728 + 384].rearrange("p (i t) -> p i t", i=3)

        scr = ring[:, 8:16, :].rearrange("p a b -> p (a b)")
        bT = scr[:, 0:1536].rearrange("p (k t) -> p k t", k=NQ)
        Eb = scr[:, 1536:3072]
        qs = scr[:, 3072:4608].rearrange("p (k t) -> p k t", k=NQ)
        ks = scr[:, 4608:6656].rearrange("p (k t) -> p k t", k=NH)
        att = scr[:, 6656:8704].rearrange("p (c h t) -> p c h t", c=NC, h=NH)
        vtok = scr[:, 8704:11776].rearrange("p (i n) -> p i n", i=3)
        kdtok = scr[:, 11776:13312].rearrange("p (c n) -> p c n", c=NC)
        Ssam = scr[:, 13312:15360].rearrange("p (u b v) -> p u b v", u=2, b=TS)
        qdec = scr[:, 15360:16384].rearrange("p (k t) -> p k t", k=NH)
        xraw = scr[:, 8704:11776].rearrange("p (i d) -> p i d", i=3)
        craw = scr[0:32, 4608:5632]
        cexp = scr[0:32, 5632:6656]
        vec = scr[0:68, 11776:11904]
        bup = scr[0:NE, 13312:15360]
        adasb = Eb[:, 0:512]
        siluT = scr[:, 11904:12160].rearrange("p (k c) -> p k c", k=KT)
        gexp = Eb[:, 512:1304].rearrange("p (i t) -> p i t", i=3)
        smask = scr[:, 6656:6784].bitcast(I32)
        tmask = scr[:, 6784:6912].bitcast(I32)
        gmask = scr[:, 6912:7040].bitcast(I32)

        vdram = nc.dram_tensor("sample_values", [TS, NH * P], F).ap()
        ydram = nc.dram_tensor("expert_rows", [(NE + EXTRA) * BLK, D], F).ap()

        w_up, w_down = a["w_up"][0], a["w_down"][0]

        block = ctx.enter_context(nc.Block())

        def state_in(u):
            if u < 4:
                return [(slice(0, P), a["state_hgrn"][0, :, u].rearrange("b k v -> k b v"))]
            return [(slice(64 * i, 64 * i + 64), a["state_gla"][0, :, 2 * (u - 4) + i].rearrange("b k v -> k b v"))
                    for i in range(2)]

        def state_out(u):
            if u < 4:
                return [(slice(0, P), o["hgs"][0, :, u].rearrange("b k v -> k b v"))]
            return [(slice(64 * i, 64 * i + 64), o["gls"][0, :, 2 * (u - 4) + i].rearrange("b k v -> k b v"))
                    for i in range(2)]

        def front_released(n):
            kind, c, s = FRONT[n]
            if kind == "ada" and s == KT - 1:
                return "ada_psum", c + 1
            if kind == "in" and s == 1:
                return "proj_psum", PROJ_AT[("proj", c, 3)] + 1
            if kind == "out" and s == 3:
                return "wo_psum", KT
            return "weights_used", FRONT_USED[n]

        def expert_released(i, q):
            if i < KT:
                e, t = -1, UP_FIRST + 4 + i - UP_FIRST if i >= UP_FIRST else i
            else:
                e, t = (i - KT) // 12, (i - KT) % 12
            if t == 11:
                return "up_done", q * UNROLL + (e + 2)
            if t == UP_FIRST + 3:
                return "down_done", q * UNROLL + (e + 1)
            plain = sum(m != KT - 1 for m in range(min(i, KT - 1) + 1)) if i < KT else (
                KT - 1 + 10 * e + t + 1 - (t > UP_FIRST + 3))
            return "weights_used", q * (10 * UNROLL) + (FRONT_PLAIN + plain)

        @block.sync
        def _(sp):
            sp.dma_start(xraw[:, 0:2, :], a["x_prompt"][0].rearrange("(i p) d -> p i d", p=P)).then_inc(sem("x_in"), 16)
            sp.dma_start(xraw[0:TS, 2, :], a["x_sample"][:, 0, :]).then_inc(sem("x_in"), 16)
            for n, (kind, c, s) in enumerate(FRONT):
                slot = FRONT_SLOT[n]
                prior = [m for m in range(n) if FRONT_SLOT[m] == slot]
                if prior:
                    name, value = front_released(prior[-1])
                    sp.wait_ge(sem(name), value)
                if kind == "ada":
                    dst, src = ring[:, slot, :], a["w_ada"][0, P * s:P * s + P, 2048 * c:2048 * c + 2048]
                elif kind == "in":
                    dst = ring[:, slot, :].rearrange("p (k n) -> p k n", k=4)
                    src = a["w_in"][0].rearrange("(k p) n -> p k n", p=P)[:, 4 * s:4 * s + 4, 512 * c:512 * c + 512]
                else:
                    dst = ring[:, slot, :].rearrange("p (k n) -> p k n", k=2)
                    src = a["w_o"][0].rearrange("(k p) n -> p k n", p=P)[:, 2 * s:2 * s + 2, :]
                sp.dma_start(dst, src).then_inc(sem(f"slot{slot}"), 16)

            def load(i, e, kind, k):
                slot = expert_slot(i)
                if kind == "up":
                    dst, src = ring[:, slot, :], w_up[bass.ds(e, 1), P * k:P * k + P, :].rearrange("a p n -> (a p) n")
                else:
                    dst = ring[:, slot, :].rearrange("p (k n) -> p k n", k=2)
                    src = w_down[bass.ds(e, 1), 2 * P * k:2 * P * k + 2 * P, :].rearrange("a (k p) n -> p (a k) n", p=P)
                sp.dma_start(dst, src).then_inc(sem(f"slot{slot}"), 16)

            def reuse(i, q=0):
                if i >= SLOTS:
                    name, value = expert_released(i - SLOTS, q)
                    sp.wait_ge(sem(name), value)
                elif expert_slot(i) < 8:
                    name, value = front_released(max(m for m in range(NF) if FRONT_SLOT[m] == expert_slot(i)))
                    sp.wait_ge(sem(name), value)
                elif i == 4:
                    sp.wait_ge(sem("heads_out"), 1)
                    sp.wait_ge(sem("states_stored0"), 96)
                    sp.wait_ge(sem("states_stored1"), 96)

            def body(e, i0, q=0):
                seq = ([("up", k) for k in range(UP_FIRST)] + [("down", s) for s in range(4)]
                       + [("up", k) for k in range(UP_FIRST, KT)])
                for t, (kind, k) in enumerate(seq):
                    reuse(i0 + t, q)
                    load(i0 + t, e + 1 if kind == "up" else e, kind, k)

            for i in range(KT):
                reuse(i)
                load(i, 0, "up", i)
            for e in range(PEEL):
                body(e, KT + 12 * e)
            with sp.Fori(0, LOOPS) as q:
                for r in range(UNROLL):
                    body(q * UNROLL + (PEEL + r), KT + 12 * (PEEL + r), q)
            for s in range(4):
                i = KT + 12 * (NE - 1) + s
                reuse(i)
                load(i, NE - 1, "down", s)
            sp.wait_ge(sem("table_ready"), 1)
            n_over = sp.value_load(table[0:1, EXTRA:EXTRA + 1], min_val=0, max_val=EXTRA)
            with sp.Fori(0, EXTRA) as j:
                with sp.If(j < n_over):
                    e = sp.value_load(table[0:1, bass.ds(j, 1)], min_val=0, max_val=NE - 1)
                    sp.wait_ge(sem("down_done"), j + NE)
                    for i in range(12):
                        load(i, e, *(("up", i) if i < KT else ("down", i - KT)))
                sp.nop()

        @block.gpsimd
        def _(pool):
            od = Order(pool, sem("pool_step"))
            g = nc.gpsimd
            od.did(g.memset(ident[:, :], 0.0))
            od.did(g.memset(ones[:, :], 1.0), sem("ones_ready"))
            od.did(g.memset(eps_col[:, :], EPS))
            od.did(g.memset(valid[:, :], 1.0))
            od.settle()
            od.did(g.affine_select(out=ident[:, :], in_=ident[:, :], compare_op=ALU.not_equal, fill=1.0, base=0,
                                   pattern=[[-1, P]], channel_multiplier=1), sem("ident_ready"))
            od.did(g.affine_select(out=before[:, :], in_=ones[:, :], compare_op=ALU.is_gt, fill=0.0, base=0,
                                   pattern=[[1, P]], channel_multiplier=-1))
            od.did(g.affine_select(out=half_mask[:, 0:1], in_=ones[:, 0:1], compare_op=ALU.is_gt, fill=0.0, base=64,
                                   pattern=[[0, 1]], channel_multiplier=-1))
            od.did(g.affine_select(out=half_mask[:, 1:2], in_=ones[:, 0:1], compare_op=ALU.is_gt, fill=0.0, base=-63,
                                   pattern=[[0, 1]], channel_multiplier=1))
            od.did(g.affine_select(out=valid[:, 2:3], in_=ones[:, 0:1], compare_op=ALU.is_gt, fill=0.0, base=TS,
                                   pattern=[[0, 1]], channel_multiplier=-1))
            od.did(g.iota(smask, pattern=[[0, P]], base=0, channel_multiplier=1))
            od.did(g.iota(tmask, pattern=[[1, P]], base=0, channel_multiplier=0))
            for dst, step, n in ((iota_slot, 1, BLK), (iota_exp, 1, NE), (base1, BLK, NE), (iota_blk, 1, EXTRA)):
                od.did(g.iota(dst[:, :], pattern=[[step, n]], base=0, channel_multiplier=0,
                              allow_small_or_imprecise_dtypes=True))
            od.settle()
            od.did(g.memset(ovbase[:, :], float(NE * BLK)), sem("const_ready"))

            for u in range(NQ):
                if u == 0 or u == 4:
                    grp = u // 4
                    pool.wait_ge(sem("aux_used"), AUX_END[("vt", grp)])
                    pool.dma_start(vdram[:, 512 * grp:512 * grp + 512],
                                   vtok[0:TS, 2, 512 * grp:512 * grp + 512]).then_inc(sem("v_dram"), 16)
                    pool.wait_ge(sem("v_dram"), 16 * grp + 16)
                if u >= 2:
                    pool.wait_ge(sem("osam_done"), u - 1)
                    pool.wait_ge(sem(f"states_stored{u % 2}"), 32 * (u // 2))
                elif u == 0:
                    pool.wait_ge(sem("bup_used"), 1)
                od.settle()
                for n, (rows, src) in enumerate(state_in(u)):
                    pool.dma_start(Ssam[rows, u % 2], src).then_inc(sem("state_in"), 16 if u >= 4 else 32)
                    if u < 4:
                        pool.dma_start(vbc[:, :, :], vdram[:, P * u:P * u + P].unsqueeze(0).to_broadcast([P, TS, P])
                                       ).then_inc(sem("vbc_in"), 32)
                    else:
                        h = 4 + 2 * (u - 4) + n
                        pool.dma_start(vbc[rows, :, :], vdram[:, P * h:P * h + P].unsqueeze(0).to_broadcast([64, TS, P])
                                       ).then_inc(sem("vbc_in"), 16)
                pool.wait_ge(sem("vbc_in"), 32 * (u + 1))
                pool.wait_ge(sem("state_in"), 32 * (u + 1))
                pool.wait_ge(sem("decay_s_ready"), 1 if u < 4 else 2)
                S = Ssam[:, u % 2]
                od.did(g.tensor_tensor(vbc[:, :, :], vbc[:, :, :],
                                       kT[:, u, TP:T].unsqueeze(2).to_broadcast([P, TS, P]), ALU.mult))
                od.link(g.tensor_tensor(S, S, decay_s[:, u, :].unsqueeze(2).to_broadcast([P, TS, P]), ALU.mult))
                od.link(g.tensor_tensor(S, S, vbc[:, :, :], ALU.add), sem("Ssam_ready"))
                for rows, dst in state_out(u):
                    pool.dma_start(dst, Ssam[rows, u % 2]).then_inc(sem(f"states_stored{u % 2}"), 16 if u >= 4 else 32)

            pool.wait_ge(sem("blocks_done"), 1)
            for i in range(3):
                n = P if i < 2 else TS
                for c in range(TOPK):
                    pool.indirect_dma_start(
                        out=ring[0:n, 4 * i + c, 0:D], out_offset=None, in_=ydram[:, :],
                        in_offset=bass.IndirectOffsetOnAxis(ap=rowk_i[0:n, i, c:c + 1], axis=0),
                    ).then_inc(sem(f"rows{i}"), 16)

        @block.scalar
        def _(act):
            od = Order(act, sem("act_step"))
            A = nc.scalar.activation
            act.wait_ge(sem("craw_zero"), 1)
            act.dma_start(craw[0:1, :], a["c_prompt"]).then_inc(sem("c_in"), 16)
            act.dma_start(craw[1:1 + TS, :], a["c_sample"]).then_inc(sem("c_in"), 16)
            for rows, src in ((slice(0, 8), a["norm1_g"][0].rearrange("(k p) -> k p", p=P)),
                              (slice(8, 16), a["norm2_g"][0].rearrange("(k p) -> k p", p=P)),
                              (slice(16, 64), a["b_ada"][0].rearrange("(k p) -> k p", p=P)),
                              (slice(64, 66), a["b_gk2"][0].rearrange("(k p) -> k p", p=P)),
                              (slice(66, 67), a["gn_hgrn"]), (slice(67, 68), a["gn_gla"])):
                act.dma_start(vec[rows, :], src).then_inc(sem("vec_in"), 16)
            act.dma_start(bup, a["b_up"][0]).then_inc(sem("bup_in"), 16)
            act.dma_start(wgr, a["w_in"][0].rearrange("(k p) n -> p k n", p=P)[:, :, 3584:3600]).then_inc(sem("gr_in"), 16)
            act.dma_start(wgk2, a["w_gk2"][0]).then_inc(sem("gr_in"), 16)
            act.dma_start(wrt[:, :, :], a["router_w"][0].rearrange("(k p) n -> p k n", p=P)).then_inc(sem("router_in"), 16)
            act.dma_start(brt[:, :], a["router_b"].to_broadcast([P, NE])).then_inc(sem("router_in"), 16)

            act.wait_ge(sem("c_in"), 32)
            od.did(A(cexp, craw, ACT.Exp, scale=-1.0), sem("cexp_ready"))
            for k in range(1, KT, 2):
                act.wait_ge(sem("xT_psum"), k + 1)
                od.did(A(xT[:, k, :], bank[:, k, 0:T], ACT.Copy), sem("xT_act"))

            def norm_square():
                od.settle()
                for k in range(0, KT, 4):
                    od.did(A(tmpT[:, k:k + 4, :], xT[:, k:k + 4, :], ACT.Square), sem("sq_ready"))

            def norm_rstd(n):
                act.wait_ge(sem("stat_psum"), n)
                od.link(A(rstd[:, :], bank[:, 0, 0:T], ACT.Ln, scale=1.0 / D, bias=eps_col[:, 0:1]))
                od.did(A(rstd[:, :], rstd[:, :], ACT.Exp, scale=-0.5), sem("rstd_ready"))

            act.wait_ge(sem("const_ready"), 1)
            act.wait_ge(sem("xT_dve"), 4)
            norm_square()
            norm_rstd(1)

            def ada_copy(r):
                act.wait_ge(sem("ada_psum"), r + 1)
                if r > 0:
                    act.wait_ge(sem("adaT_psum"), r)
                od.did(A(adasb, bank[:, 1, :], ACT.Copy), sem("ada_sb"))

            ada_copy(0)
            tA = r_tmp[:, 0:1056]
            tB = r_tmp[:, 1056:2112]
            quarter = float(64 ** -0.5)

            def proj(task):
                n = PROJ_AT[task]
                act.wait_ge(sem("proj_psum"), n + 1)
                v = bank[:, 3 + n % 3, 0:T]
                if task[0] == "low":
                    ins = A(grT, bank[0:16, 3 + n % 3, 0:T], ACT.Copy)
                elif task[0] == "y":
                    if task[1] == 0:
                        act.wait_ge(sem("q_ready"), 1)
                        act.wait_ge(sem("logk_ready"), 1)
                    ins = A(tA[:, T * task[1]:T * task[1] + T], v, ACT.Identity, bias=vecT[:, 64 + task[1]:65 + task[1]])
                else:
                    _, c, i = task
                    if c == HQ:
                        if i == 0:
                            act.wait_ge(sem("hT_ready"), 1)
                        od.did(A(tB[:, T * i:T * i + T], v, ACT.Exp, scale=-1.0))
                    if c in (HG, GG):
                        g = 4 * (c == GG) + i
                        if g == 0:
                            act.wait_ge(sem("aux_used"), AUX_END[("vt", 1)])
                        if g >= 3:
                            act.wait_ge(sem("gate_ready"), g - 2)
                        od.did(A(gexp[:, g % 3, :], v, ACT.Exp, scale=-1.0))
                        ins = A(gateT[:, g, :], v, ACT.Copy)
                    elif c == GQK and i < 2:
                        ins = A(qT[:, 4 + i, :], v, ACT.Copy, scale=quarter)
                    else:
                        dst = {HF: kT[:, i, :], HQ: qT[:, i, :], HI: vT[:, i, :],
                               GQK: kT[:, 2 + i, :] if i >= 2 else None, GV: vT[:, 4 + i, :]}[c]
                        ins = A(dst, v, ACT.Copy)
                od.settle()
                od.did(ins, sem("proj_sb"))

            levels = 0
            for task in MIDDLE:
                if task[0] in ("proj", "low", "y"):
                    proj(task)
                if task == ("proj", HQ, 3):
                    act.wait_ge(sem("negabs"), 1)
                    od.link(A(tA, tA, ACT.Exp))
                    od.did(A(tA, tA, ACT.Ln, scale=1.0, bias=1.0), sem("soft_ready"))
                if task == ("proj", HI, 3):
                    act.wait_ge(sem("logk_ready"), 1)
                    od.did(A(kT[:, 0:4, :], kT[:, 0:4, :], ACT.Exp), sem("k_ready"))
                    od.did(A(decay_s[:, 0:4, :], logf[:, 0:4, TP:T], ACT.Exp), sem("decay_s_ready"))
                if task[0] == "ada":
                    ada_copy(task[1])
                if task == ("ada", 1):
                    act.wait_ge(sem("zero_ready"), 1)
                    for j in range(EXTRA * BLK // P):
                        row = NE * BLK + P * j
                        act.dma_start(ydram[row:row + P, :].rearrange("p (h n) -> p h n", h=2),
                                      zero.unsqueeze(1).to_broadcast([P, 2, 512])).then_inc(sem("zero_stored"), 16)
                if task[0] == "lev" and task[2] > 0:
                    levels += 1
                    act.wait_ge(sem("level_sub"), levels)
                    v = Eb[:, 0:8 * P] if task[1] == 0 else Eb[:, 0:4 * P]
                    od.did(A(v, v, ACT.Exp), sem("level_exp"))
                if task == ("proj", GV, 0):
                    act.wait_ge(sem("negabs"), 2)
                    od.link(A(tB[:, 0:2 * T], tB[:, 0:2 * T], ACT.Exp))
                    od.did(A(tB[:, 0:2 * T], tB[:, 0:2 * T], ACT.Ln, scale=1.0, bias=1.0), sem("soft_ready"))
                if task == ("vt", 1):
                    act.wait_ge(sem("logf_gla"), 1)
                    od.did(A(decay_s[:, 4:6, :], logf[:, 4:6, TP:T], ACT.Exp), sem("decay_s_ready"))
                    act.wait_ge(sem("kd_sub"), 1)
                    od.did(A(kd[:, :, :], kd[:, :, :], ACT.Exp), sem("kd_exp"))
                    od.did(A(decay_c[:, :], bT[:, :, TP - 1], ACT.Exp), sem("kd_exp"))
                    od.did(A(qdec[:, 0:NQ, :], bT[:, :, P:TP], ACT.Exp), sem("kd_exp"))
                if task == ("state",):
                    act.wait_ge(sem("aux_used"), AUX_END[task])
                    act.dma_start(o["hgp"][0, 0].rearrange("h k v -> k h v"), S2[:, 0:4, :]).then_inc(sem("S2_out"), 16)
                    for i in range(2):
                        act.dma_start(o["glp"][0, 0].rearrange("(q i) k v -> i k q v", i=2)[i],
                                      S2[64 * i:64 * i + 64, 4:6, :]).then_inc(sem("S2_out"), 16)

            act.wait_ge(sem("heads_out"), 1)
            od.settle()
            for g in range(2):
                od.did(A(tmpT[:, 4 * g:4 * g + 4, :], oT[:, 4 * g:4 * g + 4, :], ACT.Square), sem("osq_ready"))
            od.settle()
            for h in range(NH):
                act.wait_ge(sem("ostat_psum"), h + 1)
                od.link(A(tmpT[:, h, :], bank[:, 3 + h % 3, 0:T], ACT.Ln, scale=1.0 / P, bias=eps_col[:, 0:1]),
                        sem("ostat_sb"))
                od.did(A(tmpT[:, h, :], tmpT[:, h, :], ACT.Exp, scale=-0.5), sem("orstd_ready"))
            act.wait_ge(sem("x1_ready"), KT)
            norm_square()
            norm_rstd(2)

            def wide(i):
                return bank[:, i:i + 2, :].rearrange("p a b -> p (a b)")

            for i in range(3):
                n = P if i < 2 else TS
                act.wait_ge(sem("x1tok_psum"), i + 1)
                od.did(A(x1tok[0:n, i, :], wide(1)[0:n, :], ACT.Copy), sem("x1tok_sb"))
            act.wait_ge(sem("h2tok_zero"), 1)
            for i in range(3):
                n = P if i < 2 else TS
                act.wait_ge(sem("h2tok_psum"), i + 1)
                od.did(A(h2tok[0:n, i, :], wide(4 + 2 * (i % 2))[0:n, :], ACT.Copy), sem("h2tok_sb"))
            act.wait_ge(sem("gate_sub"), 1)
            od.did(A(gate[:, :, :], gate[:, :, :], ACT.Exp), sem("gate_exp"))
            act.wait_ge(sem("S2_out"), 48)
            act.dma_start(fgrow, a["final_norm_g"].unsqueeze(0).to_broadcast([P, D])).then_inc(sem("fg_in"), 16)
            act.dma_start(bdn, a["b_down"][0]).then_inc(sem("bdn_in"), 16)

            def take_tokens(n, par):
                act.wait_ge(sem("gathered"), n + 1)
                act.activation(xe[:, par].rearrange("p k s -> p (k s)"), bank[:, 6, :], ACT.Copy).then_inc(sem("xe_ready"), 1)

            def take_up(n):
                act.wait_ge(sem("up_done"), n + 1)
                act.activation(us[:, 0:512], bank[:, 0, :], ACT.Copy).then_inc(sem("us_act"), 1)

            def glu_exp(n):
                act.wait_ge(sem("glu_ready"), n + 1)
                act.activation(te, tg, ACT.Exp, scale=-ALPHA).then_inc(sem("glu_exp"), 1)

            def store_rows(n, par, row, prior):
                act.wait_ge(sem("down_done"), n + 1)
                if prior is not None:
                    act.wait_ge(sem(f"rows_stored{par}"), prior)
                act.activation(ysb[:, par, :], bank[:, 5, :], ACT.Copy).then_inc(sem("ysb_ready"), 1)
                act.wait_ge(sem("ysb_ready"), n + 1)
                for half in range(2):
                    act.dma_start(ydram[bass.ds(row, BLK), 512 * half:512 * half + 512],
                                  ysb[64 * half:64 * half + 64, par, :]).then_inc(sem(f"rows_stored{par}"), 16)

            take_tokens(0, 0)
            take_up(0)
            for e in range(PEEL):
                take_tokens(e + 1, (e + 1) % 2)
                glu_exp(e)
                store_rows(e, e % 2, e * BLK, None if e < 2 else 32 * (e // 2))
                take_up(e + 1)
            with act.Fori(0, LOOPS) as q:
                for r in range(UNROLL):
                    e0 = PEEL + r
                    e = q * UNROLL + e0
                    take_tokens(e + 1, (e0 + 1) % 2)
                    glu_exp(e)
                    store_rows(e, e0 % 2, e * BLK, q * 64 + 32 * (e0 // 2))
                    take_up(e + 1)
            glu_exp(NE - 1)
            store_rows(NE - 1, 1, (NE - 1) * BLK, 32 * ((NE - 1) // 2))
            act.wait_ge(sem("rows_stored0"), 32 * (NE // 2))
            act.wait_ge(sem("rows_stored1"), 32 * (NE // 2))
            act.wait_ge(sem("table_ready"), 1)
            act.wait_ge(sem("zero_stored"), 16 * (EXTRA * BLK // P))
            n_over = act.value_load(table[0:1, EXTRA:EXTRA + 1], min_val=0, max_val=EXTRA)
            with act.Fori(0, EXTRA) as j:
                with act.If(j < n_over):
                    n = j + NE
                    take_tokens(n, 0)
                    take_up(n)
                    glu_exp(n)
                    store_rows(n, 0, n * BLK, None)
                    act.wait_ge(sem("rows_stored0"), j * 32 + 32 * (NE // 2 + 1))
                    act.sem_inc(sem("extra_stored"), 1)
                act.nop()
            act.activation(sumsq[:, 3:4], ones[:, 0:1], ACT.Copy).then_inc(sem("blocks_done"), 1)

            for i in range(3):
                n = P if i < 2 else TS
                act.wait_ge(sem("res_ready"), i + 1)
                od.link(A(ring[0:n, 12 + i, D:2 * D], ring[0:n, 12 + i, 0:D], ACT.Square, accum_out=sumsq[0:n, i:i + 1]))
                od.link(A(sumsq[0:n, i:i + 1], sumsq[0:n, i:i + 1], ACT.Ln, scale=1.0 / D, bias=eps_col[0:n, 0:1]))
                od.did(A(sumsq[0:n, i:i + 1], sumsq[0:n, i:i + 1], ACT.Exp, scale=-0.5), sem("frstd_ready"))
            for i in range(3):
                n = P if i < 2 else TS
                act.wait_ge(sem("y_ready"), i + 1)
                dst = o["yp"][0, P * i:P * i + P, :] if i < 2 else o["ys"][:, 0, :]
                act.dma_start(dst, ring[0:n, 12 + i, 0:D]).then_inc(sem("y_out"), 16)
            act.wait_ge(sem("y_out"), 48)
            act.wait_ge(sem("states_stored0"), 96)
            act.wait_ge(sem("states_stored1"), 96)
            act.wait_ge(sem("v_dram"), 32)

        @block.tensor
        def _(pe):
            mm = nc.tensor.matmul
            tr = nc.tensor.transpose
            pe.wait_ge(sem("ident_ready"), 1)
            pe.wait_ge(sem("vec_in"), 96)
            tr(bank[:, 6, 0:68], vec, ident[0:68, 0:68]).then_inc(sem("vec_psum"), 1)
            pe.wait_ge(sem("x_in"), 32)
            for k in range(KT):
                if k == 6:
                    pe.wait_ge(sem("vec_sb"), 1)
                for i in range(3):
                    n = P if i < 2 else TS
                    last = tr(bank[:, k, P * i:P * i + n], xraw[0:n, i, P * k:P * k + P], ident[0:n, 0:n])
                last.then_inc(sem("xT_psum"), 1)
            pe.wait_ge(sem("xT_act"), 4)
            pe.wait_ge(sem("xT_dve"), 4)
            pe.wait_ge(sem("silu_ready"), 1)
            for k in range(KT):
                last = tr(bank[:, 7, 32 * k:32 * k + 32], craw[:, P * k:P * k + P], ident[0:32, 0:32])
            last.then_inc(sem("silu_psum"), 1)

            def stats():
                for k in range(KT):
                    last = mm(bank[:, 0, 0:T], ones[:, :], tmpT[:, k, :], start=(k == 0), stop=(k == KT - 1))
                last.then_inc(sem("stat_psum"), 1)

            pe.wait_ge(sem("sq_ready"), 2)
            stats()
            pe.wait_ge(sem("bup_in"), 16)
            for k in range(16):
                last = tr(bank[:, 6, 32 * k:32 * k + 32], bup[:, P * k:P * k + P], ident[0:NE, 0:NE])
            last.then_inc(sem("bup_psum"), 1)

            def use_front(n):
                pe.wait_ge(sem(f"slot{FRONT_SLOT[n]}"), 16 * front_round(n))

            def ada(r):
                if r > 0:
                    pe.wait_ge(sem("ada_sb"), r)
                for k in range(KT):
                    n = FRONT_AT[("ada", r, k)]
                    use_front(n)
                    for g in range(4):
                        last = mm(bank[32 * g:32 * g + 32, 1, :], siluT[:, k, :], ring[:, FRONT_SLOT[n], 512 * g:512 * g + 512],
                                  start=(k == 0), stop=(k == KT - 1))
                    last.then_inc(sem("weights_used" if k < KT - 1 else "ada_psum"), 1)

            def ada_back(r):
                pe.wait_ge(sem("ada_sb"), r + 1)
                if r > 0:
                    pe.wait_ge(sem("mod_sb"), r)
                for i in range(4):
                    last = tr(bank[:, 2, P * i:P * i + P], adasb[:, P * i:P * i + P], ident[:, :])
                last.then_inc(sem("adaT_psum"), 1)

            pe.wait_ge(sem("silu_sb"), 1)
            ada(0)
            ada_back(0)
            pe.wait_ge(sem("hT_ready"), 1)
            pe.wait_ge(sem("bup_used"), 1)

            aux = [0]

            def aux_bank():
                b = AUX_BANK[aux[0] % 3]
                if aux[0] >= 3:
                    pe.wait_ge(sem("aux_used"), aux[0] - 2)
                aux[0] += 1
                return b

            for task in MIDDLE:
                kind = task[0]
                if kind in ("proj", "low", "y"):
                    n = PROJ_AT[task]
                    if n >= 3:
                        pe.wait_ge(sem("proj_sb"), n - 2)
                    b = 3 + n % 3
                    if kind == "proj":
                        _, c, i = task
                        for k in range(KT):
                            ld = FRONT_AT[("in", c, k // 4)]
                            if i == 0 and k % 4 == 0:
                                use_front(ld)
                            slot = FRONT_SLOT[ld]
                            last = mm(bank[:, b, 0:T], ring[:, slot, 512 * (k % 4) + P * i:512 * (k % 4) + P * i + P],
                                      hT[:, k, :], start=(k == 0), stop=(k == KT - 1))
                            if i == 3 and k == 3:
                                last.then_inc(sem("weights_used"), 1)
                        last.then_inc(sem("proj_psum"), 1)
                    elif kind == "low":
                        pe.wait_ge(sem("gr_in"), 32)
                        for k in range(KT):
                            last = mm(bank[0:16, b, 0:T], wgr[:, k, :], hT[:, k, :], start=(k == 0), stop=(k == KT - 1))
                        last.then_inc(sem("proj_psum"), 1)
                    else:
                        pe.wait_ge(sem("proj_sb"), PROJ_AT[("low",)] + 1)
                        mm(bank[:, b, 0:T], wgk2[:, P * task[1]:P * task[1] + P], grT, start=True, stop=True
                           ).then_inc(sem("proj_psum"), 1)
                elif kind == "ada":
                    ada(task[1])
                    ada_back(task[1])
                elif kind == "vt":
                    g = task[1]
                    pe.wait_ge(sem("proj_sb"), PROJ_AT[("proj", GV if g else HI, 3)] + 1)
                    for i in range(3):
                        n = P if i < 2 else TS
                        b = aux_bank()
                        for h in range(4):
                            last = tr(bank[0:n, b, P * h:P * h + P], vT[:, 4 * g + h, P * i:P * i + n], ident[:, :])
                        last.then_inc(sem("aux_psum"), 1)
                elif kind == "lev":
                    _, g, l = task
                    if l == 0:
                        if g == 0:
                            pe.wait_ge(sem("q_ready"), 1)
                            pe.wait_ge(sem("k_ready"), 1)
                        else:
                            pe.wait_ge(sem("gla_ready"), 1)
                    else:
                        pe.wait_ge(sem("level_ready"), 7 * g + l)
                    for c in range(NC):
                        b = aux_bank()
                        for h in range(4):
                            tt = slice(P * c, P * c + P)
                            if l == 0:
                                lhs = kmask[:, h, tt] if g else kT[:, h, tt]
                                rhs = qT[:, 4 + h // 2, tt] if g else qT[:, h, tt]
                            else:
                                lhs, rhs = ks[:, 4 * g + h, tt], qs[:, (4 + h // 2) if g else h, tt]
                            last = mm(bank[:, b, P * h:P * h + P], lhs, rhs, start=True, stop=True)
                        last.then_inc(sem("aux_psum"), 1)
                elif kind == "kdt":
                    pe.wait_ge(sem("kd_ready"), 1)
                    for parts in ([(0, h) for h in range(4)], [(1, h) for h in range(4)], [(0, 4), (0, 5), (1, 4), (1, 5)]):
                        b = aux_bank()
                        for n, (c, h) in enumerate(parts):
                            last = tr(bank[:, b, P * n:P * n + P], kd[:, h, P * c:P * c + P], ident[:, :])
                        last.then_inc(sem("aux_psum"), 1)
                elif kind == "state":
                    pe.wait_ge(sem("aux_used"), AUX_END[("kdt",)])
                    for c in range(NC):
                        b = aux_bank()
                        for h in range(4):
                            last = mm(bank[:, b, P * h:P * h + P], kdtok[:, c, P * h:P * h + P], vtok[:, c, P * h:P * h + P],
                                      start=True, stop=True)
                        last.then_inc(sem("aux_psum"), 1)
                    b = aux_bank()
                    for c in range(NC):
                        for q in range(2):
                            for i in range(2):
                                h = 4 + 2 * q + i
                                last = mm(bank[64 * i:64 * i + 64, b, 256 * c + P * q:256 * c + P * q + P],
                                          kdtok[:, c, 512 + P * q + 64 * i:512 + P * q + 64 * i + 64],
                                          vtok[:, c, P * h:P * h + P], start=True, stop=True)
                    last.then_inc(sem("aux_psum"), 1)
                elif kind == "out":
                    for g in range(2):
                        for c in range(NC):
                            if c == 1 and g == 0:
                                pe.wait_ge(sem("S1_ready"), 1)
                                pe.wait_ge(sem("qdec_ready"), 1)
                            if c == 0 and g == 0:
                                pe.wait_ge(sem("aux_used"), AUX_END[("lev", 1, 7)])
                            b = aux_bank()
                            for j in range(4):
                                h = 4 * g + j
                                last = mm(bank[:, b, P * j:P * j + P], vtok[:, c, P * h:P * h + P], att[:, c, h, :],
                                          start=True, stop=(c == 0))
                                if c == 1:
                                    last = mm(bank[:, b, P * j:P * j + P], S1[:, (4 + j // 2) if g else j, :],
                                              qdec[:, h, :], start=False, stop=True)
                            last.then_inc(sem("aux_psum"), 1)
                elif kind == "so":
                    u = task[1]
                    if u == 0:
                        pe.wait_ge(sem("mod_sb"), 3)
                    pe.wait_ge(sem("Ssam_ready"), u + 1)
                    for b_ in range(TS):
                        if u < 4:
                            last = mm(bank[:, 1, TS * u + b_:TS * u + b_ + 1], Ssam[:, u % 2, b_, :],
                                      qT[:, u, TP + b_:TP + b_ + 1], start=True, stop=True)
                        else:
                            c0 = TS * (4 + 2 * (u - 4)) + b_
                            last = mm(bank[:, 1, c0:c0 + TS + 1:TS], Ssam[:, u % 2, b_, :], qsam[:, u - 4, b_, :],
                                      start=True, stop=True)
                    last.then_inc(sem("osam_done"), 1)

            for h in range(NH):
                if h % 4 == 0:
                    pe.wait_ge(sem("osq_ready"), h // 4 + 1)
                if h >= 3:
                    pe.wait_ge(sem("ostat_sb"), h - 2)
                mm(bank[:, 3 + h % 3, 0:T], ones[:, :], tmpT[:, h, :], start=True, stop=True).then_inc(sem("ostat_psum"), 1)
            pe.wait_ge(sem("on_ready"), 2)
            pe.wait_ge(sem("ostat_sb"), NH)
            for m in range(KT):
                if m >= 3:
                    pe.wait_ge(sem("x1_ready"), m - 2)
                for k in range(KT):
                    ld = FRONT_AT[("out", 0, k // 2)]
                    if m == 0 and k % 2 == 0:
                        use_front(ld)
                    last = mm(bank[:, 3 + m % 3, 0:T], ring[:, FRONT_SLOT[ld], D * (k % 2) + P * m:D * (k % 2) + P * m + P],
                              oT[:, k, :], start=(k == 0), stop=(k == KT - 1))
                    if m == KT - 1 and k % 2 == 1 and k < KT - 1:
                        last.then_inc(sem("weights_used"), 1)
                last.then_inc(sem("wo_psum"), 1)
            pe.wait_ge(sem("sq_ready"), 4)
            stats()
            for i in range(3):
                n = P if i < 2 else TS
                if i > 0:
                    pe.wait_ge(sem("x1tok_sb"), i)
                for k in range(KT):
                    last = tr(bank[0:n, 1 + k // 4, P * (k % 4):P * (k % 4) + P], xT[:, k, P * i:P * i + n], ident[:, :])
                last.then_inc(sem("x1tok_psum"), 1)
            pe.wait_ge(sem("hT_ready"), 2)
            pe.wait_ge(sem("router_in"), 32)
            for i in range(3):
                n = P if i < 2 else TS
                for k in range(KT):
                    last = mm(bank[0:n, 3, NE * i:NE * i + NE], h2T[:, k, P * i:P * i + n], wrt[:, k, :],
                              start=(k == 0), stop=(k == KT - 1))
            last.then_inc(sem("logit_psum"), 1)
            for i in range(3):
                n = P if i < 2 else TS
                if i == 2:
                    pe.wait_ge(sem("h2tok_sb"), 1)
                b = 4 + 2 * (i % 2)
                for k in range(KT):
                    last = tr(bank[0:n, b + k // 4, P * (k % 4):P * (k % 4) + P], h2T[:, k, P * i:P * i + n], ident[:, :])
                last.then_inc(sem("h2tok_psum"), 1)
            pe.wait_ge(sem("picked_ready"), 1)
            pe.wait_ge(sem("x1tok_sb"), 3)
            for i in range(3):
                for j in range(i + 1):
                    mm(bank[:, 2, NE * i:NE * i + NE], before[:, :] if j == i else ones[:, :], picked[:, j, :],
                       start=(j == 0), stop=(j == i))
            for j in range(3):
                last = mm(bank[:, 2, 3 * NE:4 * NE], ones[:, :], picked[:, j, :], start=(j == 0), stop=(j == 2))
            last.then_inc(sem("rank_psum"), 1)

            def gather(n):
                pe.wait_ge(sem("pick_ready"), n + 1)
                if isinstance(n, int) and n == 0:
                    pe.wait_ge(sem("h2tok_sb"), 3)
                else:
                    pe.wait_ge(sem("xe_ready"), n)
                for k in range(KT):
                    for i in range(3):
                        last = mm(bank[:, 6, BLK * k:BLK * k + BLK], h2tok[:, i, P * k:P * k + P], pick[:, i, :],
                                  start=(i == 0), stop=(i == 2))
                last.then_inc(sem("gathered"), 1)

            def up(par, k0, k1, loads, rounds):
                for k in range(k0, k1):
                    slot = loads(k)
                    pe.wait_ge(sem(f"slot{slot}"), rounds(k))
                    for b in range(2):
                        for half in range(2):
                            col = 1024 * b + 512 * half
                            last = mm(bank[64 * half:64 * half + 64, b, :], xe[:, par, k, :], ring[:, slot, col:col + 512],
                                      start=(k == 0), stop=(k == KT - 1))
                    if k == KT - 1:
                        last.then_inc(sem("up_done"), 1)
                    else:
                        last.then_inc(sem("weights_used"), 1)

            def back(n):
                pe.wait_ge(sem("us_act"), n + 1)
                pe.wait_ge(sem("us_dve"), n + 1)
                if not (isinstance(n, int) and n == 0):
                    pe.wait_ge(sem("act_ready"), n)
                for b in range(2):
                    for j in range(4):
                        last = tr(bank[:, 2 + b, P * j:P * j + P], us[:, 512 * b + P * j:512 * b + P * j + P], ident[:, :])
                last.then_inc(sem("u_psum"), 1)

            def down(n, loads, rounds):
                pe.wait_ge(sem("act_ready"), n + 1)
                if not (isinstance(n, int) and n == 0):
                    pe.wait_ge(sem("ysb_ready"), n)
                for s in range(4):
                    slot = loads(s)
                    pe.wait_ge(sem(f"slot{slot}"), rounds(s))
                    for kk in range(2):
                        k = 2 * s + kk
                        for half in range(2):
                            last = mm(bank[64 * half:64 * half + 64, 5, :], actT[:, k, :],
                                      ring[:, slot, D * kk + 512 * half:D * kk + 512 * half + 512],
                                      start=(k == 0), stop=(k == KT - 1))
                    if s == 3:
                        last.then_inc(sem("down_done"), 1)
                    else:
                        last.then_inc(sem("weights_used"), 1)

            def at_load(i, q=0):
                slot = expert_slot(i)
                return slot, q * 48 + 16 * (FRONT_FILLS[slot] + i // SLOTS + 1)

            def loads_of(i0, q=0):
                return (lambda t: at_load(i0 + t, q)[0]), (lambda t: at_load(i0 + t, q)[1])

            gather(0)
            pe.wait_ge(sem("xe_ready"), 1)
            lo, ro = loads_of(0)
            pe.wait_ge(sem("rank_sb"), 1)
            up(0, 0, KT, lo, ro)

            late = [0]

            def late_bank():
                b = (4, 7)[late[0] % 2]
                if late[0] >= 2:
                    pe.wait_ge(sem("late_used"), late[0] - 1)
                late[0] += 1
                return b

            for half in range(2):
                b = late_bank()
                for k in range(4):
                    last = mm(bank[:, b, P * k:P * k + P], modT[:, 40 + 4 * half + k, 0:1].to_broadcast([P, P]), ident[:, :],
                              start=True, stop=True)
                last.then_inc(sem("late_psum"), 1)
            for half in range(2):
                b = late_bank()
                for k in range(4):
                    last = tr(bank[0:TS, b, P * k:P * k + P], modT[:, 40 + 4 * half + k, 1:9], ident[:, :])
                last.then_inc(sem("late_psum"), 1)
            pe.wait_ge(sem("gateE_ready"), 1)
            b = late_bank()
            for i in range(3):
                last = tr(bank[0:NE, b, P * i:P * i + P], gateE[:, i, :], ident[:, :])
            last.then_inc(sem("late_psum"), 1)
            pe.wait_ge(sem("late_used"), 5)
            pe.wait_ge(sem("bdn_in"), 16)
            for i in range(3):
                for half in range(2):
                    b = late_bank()
                    mm(bank[:, b, :], gateTok[0:NE, i, :], bdn[:, 512 * half:512 * half + 512], start=True, stop=True
                       ).then_inc(sem("late_psum"), 1)

            def body(e, par, i0, q=0):
                gather(e + 1)
                back(e)
                pe.wait_ge(sem("xe_ready"), e + 2)
                lo, ro = loads_of(i0, q)
                up(1 - par, 0, UP_FIRST, lo, ro)
                lo, ro = loads_of(i0 + UP_FIRST, q)
                down(e, lo, ro)
                lo, ro = loads_of(i0 + 4, q)
                up(1 - par, UP_FIRST, KT, lo, ro)

            for e in range(PEEL):
                body(e, e % 2, 8 + 12 * e)
            with pe.Fori(0, LOOPS) as q:
                for r in range(UNROLL):
                    body(q * UNROLL + (PEEL + r), (PEEL + r) % 2, 8 + 12 * (PEEL + r), q)
            back(NE - 1)
            lo, ro = loads_of(8 + 12 * (NE - 1))
            down(NE - 1, lo, ro)

            total = 12 * NE
            full = [16 * (FRONT_FILLS[expert_slot(i)] + sum(expert_slot(m) == expert_slot(i) for m in range(total)))
                    for i in range(12)]
            pe.wait_ge(sem("table_ready"), 1)
            n_over = pe.value_load(table[0:1, EXTRA:EXTRA + 1], min_val=0, max_val=EXTRA)
            with pe.Fori(0, EXTRA) as j:
                with pe.If(j < n_over):
                    n = j + NE
                    gather(n)
                    pe.wait_ge(sem("xe_ready"), n + 1)
                    up(0, 0, KT, expert_slot, lambda k: j * 16 + (full[k] + 16))
                    back(n)
                    down(n, lambda s: expert_slot(8 + s), lambda s: j * 16 + (full[8 + s] + 16))
                    pe.nop()
                pe.nop()

        @block.vector
        def _(dve):
            od = Order(dve, sem("dve_step"))
            v = nc.vector
            TT, TSC, STT = v.tensor_tensor, v.tensor_scalar, v.scalar_tensor_tensor
            od.did(v.memset(craw, 0.0), sem("craw_zero"))
            od.did(v.memset(logit[:, :, :], 0.0))
            od.did(v.memset(zero, 0.0), sem("zero_ready"))
            dve.wait_ge(sem("vec_psum"), 1)
            od.did(v.tensor_copy(vecT[:, :], bank[:, 6, 0:68]), sem("vec_sb"))
            for k in range(0, KT, 2):
                dve.wait_ge(sem("xT_psum"), k + 1)
                od.did(v.tensor_copy(xT[:, k, :], bank[:, k, 0:T]), sem("xT_dve"))
            dve.wait_ge(sem("cexp_ready"), 1)
            od.link(TSC(cexp, cexp, 1.0, None, ALU.add))
            od.link(v.reciprocal(cexp, cexp))
            od.did(TT(craw, craw, cexp, ALU.mult), sem("silu_ready"))
            dve.wait_ge(sem("const_ready"), 1)
            od.link(TT(gmask, tmask, smask, ALU.is_gt))
            od.link(TT(smask, smask, tmask, ALU.bitwise_xor))
            od.link(TT(smask, smask, gmask, ALU.mult))
            for n, m in enumerate(LEVELS):
                od.did(TSC(level_mask[:, n, :], smask, float(m), None, ALU.is_ge))
            dve.wait_ge(sem("silu_psum"), 1)
            od.did(v.tensor_copy(siluT.rearrange("p k c -> p (k c)"), bank[:, 7, 0:256]), sem("silu_sb"))
            dve.wait_ge(sem("bup_psum"), 1)
            od.did(v.tensor_copy(bupT[:, :, :].rearrange("p k e -> p (k e)"), bank[:, 6, :]), sem("bup_used"))

            def mod_add(r):
                dve.wait_ge(sem("adaT_psum"), r + 1)
                od.did(TT(modT[:, 16 * r:16 * r + 16, :].rearrange("p (g i) t -> p g i t", g=4),
                          bank[:, 2, :].rearrange("p (i g c) -> p g i c", i=4, g=4)[:, :, :, 0:9],
                          vecT[:, 16 + 16 * r:32 + 16 * r].rearrange("p (g i) -> p g i", g=4).unsqueeze(3)
                          .to_broadcast([P, 4, 4, 9]), ALU.add), sem("mod_sb"))

            def mod_scale(dst, sc, g):
                od.link(STT(dst[:, :, :], modT[:, sc:sc + 8, :], 1.0,
                            vecT[:, g:g + 8].unsqueeze(2).to_broadcast([P, KT, 9]), ALU.add, ALU.mult))

            def norm_mod(dst, scale, sh):
                dve.wait_ge(sem("rstd_ready"), 1 if scale is scale1 else 2)
                od.link(TT(dst, xT, rstd[:, :].unsqueeze(1).to_broadcast([P, KT, T]), ALU.mult))
                for k in range(KT):
                    od.did(TSC(dst[:, k, 0:TP], dst[:, k, 0:TP], scale[:, k, 0:1], modT[:, sh + k, 0:1], ALU.mult, ALU.add))
                od.link(TT(dst[:, :, TP:T], dst[:, :, TP:T], scale[:, :, 1:9], ALU.mult))
                od.did(TT(dst[:, :, TP:T], dst[:, :, TP:T], modT[:, sh:sh + 8, 1:9], ALU.add), sem("hT_ready"))

            mod_add(0)
            od.settle()
            mod_scale(scale1, 8, 0)
            norm_mod(hT, scale1, 0)
            tA = r_tmp[:, 0:1056]
            tB = r_tmp[:, 1056:2112]
            kflat = r_k[:, 0:1056]
            lflat = r_qf[:, 1584:1584 + 1056]

            aux = [0]

            def aux_in():
                b = AUX_BANK[aux[0] % 3]
                aux[0] += 1
                dve.wait_ge(sem("aux_psum"), aux[0])
                return b

            def scans(tiles):
                for n in tiles:
                    for c in range(NC):
                        od.did(v.tensor_tensor_scan(bT[:, n, P * c:P * c + P], ones[:, :], logf[:, n, P * c:P * c + P],
                                                    0.0, ALU.mult, ALU.add))
                od.settle()

            def level_sub(g, m):
                n0, nt = (0, 4) if g == 0 else (4, 2)
                b = bT[:, n0:n0 + nt, :].rearrange("p n (q f i) -> p (n q) f i", f=2, i=m)
                pairs = nt * TP // (2 * m)
                ref = b[:, :, 0, m - 1:m].to_broadcast([P, pairs, m])
                Eq = Eb[:, 0:nt * P].rearrange("p (q i) -> p q i", i=m)
                Ek = Eb[:, nt * P:2 * nt * P].rearrange("p (q i) -> p q i", i=m)
                od.did(TT(Eq, b[:, :, 1, :], ref, ALU.subtract))
                od.settle()
                od.did(TT(Ek, ref, b[:, :, 0, :], ALU.subtract), sem("level_sub"))

            def level_mul(g, m):
                n0, nt = (0, 4) if g == 0 else (4, 2)

                def split(x, n):
                    return x.rearrange("p n (q f i) -> p n q f i", f=2, i=m)

                Eq = Eb[:, 0:nt * P].rearrange("p (n q i) -> p n q i", n=nt, i=m)
                Ek = Eb[:, nt * P:2 * nt * P].rearrange("p (n q i) -> p n q i", n=nt, i=m)
                od.did(TT(split(qs[:, n0:n0 + nt, :], nt)[:, :, :, 1, :], split(qT[:, n0:n0 + nt, 0:TP], nt)[:, :, :, 1, :],
                          Eq, ALU.mult))
                if g == 0:
                    od.settle()
                    od.did(TT(split(ks[:, 0:4, :], 4)[:, :, :, 0, :], split(kT[:, 0:4, 0:TP], 4)[:, :, :, 0, :], Ek, ALU.mult),
                           sem("level_ready"))
                else:
                    for h in range(4):
                        if h == 3:
                            od.settle()
                        od.did(TT(split(ks[:, 4 + h:5 + h, :], 1)[:, 0, :, 0, :], split(kmask[:, h:h + 1, 0:TP], 1)[:, 0, :, 0, :],
                                  Ek[:, h // 2], ALU.mult), sem("level_ready") if h == 3 else None)

            def level_take(g, l):
                for c in range(NC):
                    b = aux_in()
                    dst = att[:, c, 4 * g:4 * g + 4, :]
                    src = bank[:, b, :].rearrange("p (h t) -> p h t", h=4)
                    if l == 0:
                        od.did(TT(dst, src, ident[:, :].unsqueeze(1).to_broadcast([P, 4, P]), ALU.mult), sem("aux_used"))
                    else:
                        od.did(v.copy_predicated(dst, level_mask[:, l - 1, :].unsqueeze(1).to_broadcast([P, 4, P]), src),
                               sem("aux_used"))
                od.settle()

            for task in MIDDLE:
                kind = task[0]
                if task == ("proj", HF, 3):
                    dve.wait_ge(sem("proj_sb"), PROJ_AT[task] + 1)
                    od.did(STT(tA, kflat, -1.0, kflat, ALU.mult, ALU.min), sem("negabs"))
                if task == ("proj", HQ, 3):
                    dve.wait_ge(sem("proj_sb"), PROJ_AT[task] + 1)
                    od.settle()
                    od.link(TSC(tB, tB, 1.0, None, ALU.add))
                    od.link(v.reciprocal(tB, tB))
                    od.did(TT(qT[:, 0:4, :], qT[:, 0:4, :], tB.rearrange("p (k t) -> p k t", k=4), ALU.mult), sem("q_ready"))
                    dve.wait_ge(sem("soft_ready"), 1)
                    od.link(STT(lflat, kflat, 0.0, tA, ALU.min, ALU.subtract))
                    od.link(TT(kflat, lflat, kflat, ALU.subtract), sem("logk_ready"))
                    scans(range(4))
                if task == ("ada", 1):
                    mod_add(1)
                if task == ("ada", 2):
                    mod_add(2)
                    od.settle()
                    mod_scale(scale2, 32, 8)
                    od.did(v.memset(qs[:, :, :], 0.0))
                    od.did(v.memset(ks[:, :, :], 0.0))
                    od.settle()
                    dve.wait_ge(sem("ada_sb"), 3)
                    dve.wait_ge(sem("adaT_psum"), 3)
                    dve.wait_ge(sem("k_ready"), 1)
                    level_sub(0, LEVELS[0])
                if kind == "vt":
                    g = task[1]
                    for i in range(3):
                        n = P if i < 2 else TS
                        b = aux_in()
                        od.did(v.tensor_copy(vtok[0:n, i, 512 * g:512 * g + 512], bank[0:n, b, :]), sem("aux_used"))
                    od.settle()
                if kind == "lev":
                    _, g, l = task
                    if l > 0:
                        dve.wait_ge(sem("level_exp"), 7 * g + l)
                        od.settle()
                        level_mul(g, LEVELS[l - 1])
                        od.settle()
                        if l < 7:
                            level_sub(g, LEVELS[l])
                    level_take(g, l)
                if task == ("y", 1):
                    dve.wait_ge(sem("proj_sb"), PROJ_AT[task] + 1)
                    od.link(STT(tB[:, 0:2 * T], tA[:, 0:2 * T], -1.0, tA[:, 0:2 * T], ALU.mult, ALU.min), sem("negabs"))
                if task == ("proj", GV, 1):
                    dve.wait_ge(sem("soft_ready"), 2)
                    lg = r_qf[:, 1584 + 1056:3168]
                    od.link(STT(lg, tA[:, 0:2 * T], 0.0, tB[:, 0:2 * T], ALU.min, ALU.subtract))
                    od.link(TSC(lg, lg, 1.0 / 16.0, None, ALU.mult), sem("logf_gla"))
                    scans(range(4, 6))
                    for h in range(4):
                        od.did(TSC(kmask[:, h, :], kT[:, 4 + h // 2, :], half_mask[:, h % 2:h % 2 + 1], None, ALU.mult))
                    for n in range(4):
                        q, i = n // 2, n % 2
                        if n == 3:
                            od.settle()
                        od.did(TSC(qsam[:, q, :, i], qT[:, 4 + q, TP:T], half_mask[:, i:i + 1], None, ALU.mult),
                               sem("gla_ready") if n == 3 else None)
                    b4 = bT[:, :, :].rearrange("p n (c t) -> p (n c) t", c=NC)
                    od.did(TT(kd[:, :, :].rearrange("p n (c t) -> p (n c) t", c=NC),
                              b4[:, :, P - 1:P].to_broadcast([P, NQ * NC, P]), b4, ALU.subtract), sem("kd_sub"))
                    level_sub(1, LEVELS[0])
                if task == ("proj", HG, 1):
                    dve.wait_ge(sem("kd_exp"), 3)
                    od.settle()
                    od.did(TT(kd[:, :, :], kd[:, :, :], kT[:, :, 0:TP], ALU.mult), sem("kd_ready"))
                    od.link(TT(qdec[:, 0:NQ, :], qdec[:, 0:NQ, :], qT[:, :, P:TP], ALU.mult))
                    for dst, src, i in ((6, 5, 0), (7, 5, 1), (5, 4, 1), (4, 4, 0)):
                        od.link(TSC(qdec[:, dst, :], qdec[:, src, :], half_mask[:, i:i + 1], None, ALU.mult),
                                sem("qdec_ready") if dst == 4 else None)
                if kind == "kdt":
                    for n in range(3):
                        b = aux_in()
                        if n < 2:
                            ins = v.tensor_copy(kdtok[:, n, 0:512], bank[:, b, :])
                        else:
                            ins = v.tensor_copy(kdtok[:, :, 512:768], bank[:, b, :].rearrange("p (c n) -> p c n", c=NC))
                        od.did(ins, sem("aux_used"))
                if kind == "proj" and task[1] in (HG, GG):
                    g = 4 * (task[1] == GG) + task[2]
                    dve.wait_ge(sem("proj_sb"), PROJ_AT[task] + 1)
                    ge = gexp[:, g % 3, :]
                    gn = vecT[:, 66 + g // 4:67 + g // 4]
                    od.link(TSC(ge, ge, 1.0, None, ALU.add))
                    od.link(v.reciprocal(ge, ge))
                    od.link(STT(gateT[:, g, :], gateT[:, g, :], gn, ge, ALU.mult, ALU.mult), sem("gate_ready"))
                if kind == "state":
                    dve.wait_ge(sem("zero_stored"), 16 * (EXTRA * BLK // P))
                    b = aux_in()
                    od.did(v.tensor_copy(S1[:, 0:4, :].rearrange("p h v -> p (h v)"), bank[:, b, :]), sem("aux_used"))
                    b1 = aux_in()
                    b2 = aux_in()
                    od.settle()
                    od.link(v.tensor_copy(S1[:, 4:6, :].rearrange("p h v -> p (h v)"), bank[:, b2, 0:256]), sem("S1_ready"))
                    od.link(TT(S2, S1, decay_c[:, :].unsqueeze(2).to_broadcast([P, NQ, P]), ALU.mult))
                    od.did(TT(S2[:, 0:4, :], S2[:, 0:4, :], bank[:, b1, :].rearrange("p (h v) -> p h v", h=4), ALU.add),
                           sem("aux_used"))
                    od.settle()
                    od.did(TT(S2[:, 4:6, :], S2[:, 4:6, :], bank[:, b2, 256:512].rearrange("p (h v) -> p h v", h=2), ALU.add),
                           sem("aux_used"))
                if kind == "out":
                    for g in range(2):
                        for c in range(NC):
                            b = aux_in()
                            od.did(v.tensor_copy(oT[:, 4 * g:4 * g + 4, P * c:P * c + P],
                                                 bank[:, b, :].rearrange("p (h t) -> p h t", h=4)), sem("aux_used"))
            dve.wait_ge(sem("osam_done"), NQ)
            od.settle()
            od.did(v.tensor_copy(oT[:, :, TP:T], bank[:, 1, 0:64].rearrange("p (h b) -> p h b", h=NH)), sem("heads_out"))
            od.settle()
            for g in range(2):
                dve.wait_ge(sem("orstd_ready"), 4 * g + 4)
                hh = slice(4 * g, 4 * g + 4)
                od.link(TT(oT[:, hh, :], oT[:, hh, :], tmpT[:, hh, :], ALU.mult))
                od.did(TT(oT[:, hh, :], oT[:, hh, :], gateT[:, hh, :], ALU.mult), sem("on_ready"))
            od.settle()
            for m in range(KT):
                dve.wait_ge(sem("wo_psum"), m + 1)
                src = bank[:, 3 + m % 3, :]
                od.did(STT(xT[:, m, 0:TP], src[:, 0:TP], modT[:, 16 + m, 0:1], xT[:, m, 0:TP], ALU.mult, ALU.add))
                od.did(TT(rstd[:, 0:TS], src[:, TP:T], modT[:, 16 + m, 1:9], ALU.mult))
                od.settle()
                od.link(TT(xT[:, m, TP:T], xT[:, m, TP:T], rstd[:, 0:TS], ALU.add), sem("x1_ready"))
            od.did(v.memset(h2tok[:, 2, :], 0.0), sem("h2tok_zero"))
            dve.wait_ge(sem("Ssam_ready"), NQ)
            norm_mod(h2T, scale2, 24)
            od.settle()

            dve.wait_ge(sem("logit_psum"), 1)
            od.did(TT(logit[:, 0:2, :], bank[:, 3, 0:2 * NE].rearrange("p (i e) -> p i e", i=2),
                      brt[:, :].unsqueeze(1).to_broadcast([P, 2, NE]), ALU.add))
            od.link(TT(logit[0:TS, 2, :], bank[0:TS, 3, 2 * NE:3 * NE], brt[0:TS, :], ALU.add))
            for i in range(3):
                od.did(v.max(top_v[:, i, :], logit[:, i, :]))
            od.settle()
            for i in range(3):
                od.did(v.max_index(top_i[:, i, :], top_v[:, i, :], logit[:, i, :]))
            od.settle()
            od.did(TT(gate[:, :, :], top_v[:, :, 0:TOPK], top_v[:, :, 0:1].to_broadcast([P, 3, TOPK]), ALU.subtract),
                   sem("gate_sub"))
            od.link(v.tensor_copy(top_f[:, :, :], top_i[:, :, 0:TOPK]))
            for i in range(3):
                od.did(TT(onehot[:, i], iota_exp[:, :].unsqueeze(1).to_broadcast([P, TOPK, NE]),
                          top_f[:, i, :].unsqueeze(2).to_broadcast([P, TOPK, NE]), ALU.is_equal))
            od.settle()
            od.link(TSC(onehot[:, 2], onehot[:, 2], valid[:, 2:3], None, ALU.mult))
            od.link(v.tensor_reduce(picked[:, :, :], onehot.rearrange("p i c e -> p i e c"), axis=AX.X, op=ALU.add),
                    sem("picked_ready"))
            dve.wait_ge(sem("gate_exp"), 1)
            od.link(v.tensor_reduce(gsum[:, :], gate[:, :, :], axis=AX.X, op=ALU.add))
            od.link(v.reciprocal(gsum[:, :], gsum[:, :]))
            od.link(TT(gate[:, :, :], gate[:, :, :], gsum[:, :].unsqueeze(2).to_broadcast([P, 3, TOPK]), ALU.mult))
            dve.wait_ge(sem("rank_psum"), 1)
            rk = bank[:, 2, 0:3 * NE].rearrange("p (i e) -> p i e", i=3)
            od.did(v.tensor_copy(cnt[:, :], bank[:, 2, 3 * NE:4 * NE]))
            od.link(STT(rank[:, :, :], rk, 1.0, picked[:, :, :], ALU.add, ALU.mult))
            od.link(TSC(rank[:, :, :], rank[:, :, :], -1.0, None, ALU.add), sem("rank_sb"))

            def make_pick(n):
                TT(pick, iota_slot[:, :].unsqueeze(1).to_broadcast([P, 3, BLK]),
                   rank[:, :, bass.ds(n, 1)].to_broadcast([P, 3, BLK]), ALU.is_equal).then_inc(sem("pick_ready"), 1)

            make_pick(0)
            od.did(TSC(nblk[:, :], cnt[:, :], float(BLK), None, ALU.is_gt))
            for m in (2, 3, 4):
                od.settle()
                od.link(TSC(tmpe[:, :], cnt[:, :], float(BLK * m), None, ALU.is_gt))
                od.did(TT(nblk[:, :], nblk[:, :], tmpe[:, :], ALU.add))
            od.settle()
            od.link(v.tensor_tensor_scan(cumb[:, :], ones[:, 0:NE], nblk[:, :], 0.0, ALU.mult, ALU.add))
            od.link(TT(tmpe[:, :], cumb[:, :], nblk[:, :], ALU.subtract))
            od.link(TSC(tmpe[:, :], tmpe[:, :], float(BLK), float(NE * BLK - BLK), ALU.mult, ALU.add))
            od.link(TT(tmpe[:, :], tmpe[:, :], base1[:, :], ALU.subtract))
            od.link(TSC(over, rank[:, :, :], float(BLK), None, ALU.is_ge))
            od.link(TT(over, over, tmpe[:, :].unsqueeze(1).to_broadcast([P, 3, NE]), ALU.mult))
            od.link(TT(rowid[:, :, :], over, base1[:, :].unsqueeze(1).to_broadcast([P, 3, NE]), ALU.add))
            od.link(TT(rowid[:, :, :], rowid[:, :, :], rank[:, :, :], ALU.add))
            od.link(STT(rowid[:, :, :], rowid[:, :, :], 1.0, picked[:, :, :], ALU.add, ALU.mult))
            od.link(TSC(rowid[:, :, :], rowid[:, :, :], -1.0, None, ALU.add))
            for i in range(3):
                od.did(TT(weighted[:, i], onehot[:, i], rowid[:, i, :].unsqueeze(1).to_broadcast([P, TOPK, NE]), ALU.mult))
            od.settle()
            od.link(v.tensor_reduce(rowk[:, :, :], weighted, axis=AX.X, op=ALU.add))
            od.link(v.tensor_copy(rowk_i[:, :, :], rowk[:, :, :]))
            for j in range(EXTRA):
                od.did(TSC(ovw[:, j, :], cumb[:, :], float(j), None, ALU.is_le))
            od.settle()
            od.link(v.tensor_reduce(table_f[:, 0:EXTRA], ovw, axis=AX.X, op=ALU.add))
            od.link(TSC(table_f[:, 0:EXTRA], table_f[:, 0:EXTRA], float(NE - 1), None, ALU.min))
            od.link(v.tensor_copy(table_f[:, EXTRA:EXTRA + 1], cumb[:, NE - 1:NE]))
            od.link(v.tensor_copy(table[:, :], table_f[:, :]), sem("table_ready"))
            for i in range(3):
                od.did(TT(weighted[:, i], onehot[:, i], gate[:, i, :].unsqueeze(2).to_broadcast([P, TOPK, NE]), ALU.mult))
            od.settle()
            od.link(v.tensor_reduce(gateE[:, :, :], weighted.rearrange("p i c e -> p i e c"), axis=AX.X, op=ALU.add),
                    sem("gateE_ready"))

            def take_up(n):
                dve.wait_ge(sem("up_done"), n + 1)
                v.tensor_copy(us[:, 512:1024], bank[:, 1, :]).then_inc(sem("us_dve"), 1)

            take_up(0)
            late = [0]

            def late_in():
                b = (4, 7)[late[0] % 2]
                late[0] += 1
                dve.wait_ge(sem("late_psum"), late[0])
                return b

            for i in range(2):
                n = P if i == 0 else TS
                for half in range(2):
                    b = late_in()
                    od.did(v.tensor_copy(g2row[0:n, i, 512 * half:512 * half + 512], bank[0:n, b, :]), sem("late_used"))
            b = late_in()
            od.link(v.tensor_copy(gateTok[0:NE, :, :].rearrange("p i t -> p (i t)"), bank[0:NE, b, 0:384]), sem("late_used"))
            for i in range(3):
                n = P if i < 2 else TS
                for half in range(2):
                    b = late_in()
                    cols = slice(512 * half, 512 * half + 512)
                    od.link(TT(r_tmp[0:n, 1024:1536], bank[0:n, b, :], g2row[0:n, i // 2, cols], ALU.mult), sem("late_used"))
                    od.link(TT(x1tok[0:n, i, cols], x1tok[0:n, i, cols], r_tmp[0:n, 1024:1536], ALU.add))

            chain_at = [od.count[id(od.chain)]]

            def glu(n, bias, link):
                dve.wait_ge(sem("u_psum"), n + 1)

                def with_bias(dst, b):
                    return TT(dst.rearrange("p (j h s) -> p j h s", j=4, h=2),
                              bank[:, 2 + b, :].rearrange("p (j h s) -> p j h s", j=4, h=2),
                              bias(b).to_broadcast([P, 4, 2, BLK]), ALU.add)

                link(with_bias(tg, 0))
                v.tensor_scalar(tg, tg, LIMIT, None, ALU.min).then_inc(sem("glu_ready"), 1)
                link(with_bias(tl, 1))
                link(TSC(tl, tl, LIMIT, -LIMIT, ALU.min, ALU.max))
                dve.wait_ge(sem("glu_ready"), n + 1)
                link(STT(tl, tl, 1.0, tg, ALU.add, ALU.mult))
                dve.wait_ge(sem("glu_exp"), n + 1)
                link(TSC(te, te, 1.0, None, ALU.add))
                link(v.reciprocal(te, te))
                TT(actT[:, :, :].rearrange("p (h j) s -> p j h s", h=2), tl.rearrange("p (j h s) -> p j h s", j=4, h=2),
                   te.rearrange("p (j h s) -> p j h s", j=4, h=2), ALU.mult).then_inc(sem("act_ready"), 1)

            GLU_LINKS = 6

            def linker(base):
                k = [0]

                def link(ins):
                    k[0] += 1
                    ins.then_inc(od.chain, 1)
                    dve.wait_ge(od.chain, base + k[0])
                return link

            def bias_at(e):
                return lambda b: bupT[:, 8 * b:8 * b + 8, bass.ds(e, 1)].rearrange("p (h j) e -> p j h e", h=2)

            def body(e, par, base):
                dve.wait_ge(sem("gathered"), e + 1)
                make_pick(e + 1)
                glu(e, bias_at(e), linker(base))
                take_up(e + 1)

            base0 = chain_at[0]
            for e in range(PEEL):
                body(e, e % 2, base0 + GLU_LINKS * e)
            with dve.Fori(0, LOOPS) as q:
                for r in range(UNROLL):
                    e = q * UNROLL + (PEEL + r)
                    base = q * (GLU_LINKS * UNROLL) + (base0 + GLU_LINKS * (PEEL + r))
                    body(e, (PEEL + r) % 2, base)
            glu(NE - 1, bias_at(NE - 1), linker(base0 + GLU_LINKS * (NE - 1)))

            base1_ = base0 + GLU_LINKS * NE
            n_over = dve.value_load(table[0:1, EXTRA:EXTRA + 1], min_val=0, max_val=EXTRA)
            LOOP_LINKS = GLU_LINKS + 2
            with dve.Fori(0, EXTRA) as j:
                with dve.If(j < n_over):
                    n = j + NE
                    e = dve.value_load(table[0:1, bass.ds(j, 1)], min_val=0, max_val=NE - 1)
                    link = linker(j * LOOP_LINKS + base1_)
                    link(TSC(ovr[:, :], rowid[:, :, bass.ds(e, 1)].rearrange("p i e -> p (i e)"), ovbase[:, 0:1], None,
                             ALU.subtract))
                    link(TSC(ovbase[:, :], ovbase[:, :], float(BLK), None, ALU.add))
                    TT(pick, iota_slot[:, :].unsqueeze(1).to_broadcast([P, 3, BLK]),
                       ovr[:, :].unsqueeze(2).to_broadcast([P, 3, BLK]), ALU.is_equal).then_inc(sem("pick_ready"), 1)
                    take_up(n)
                    glu(n, bias_at(e), link)
                    dve.nop()
                dve.nop()

            od2 = Order(dve, sem("tail_step"))
            for i in range(3):
                n = P if i < 2 else TS
                dve.wait_ge(sem(f"rows{i}"), 16 * TOPK)
                y = ring[0:n, 12 + i, 0:D]
                od2.link(TSC(y, ring[0:n, 4 * i, 0:D], gate[0:n, i, 0:1], None, ALU.mult))
                for c in range(1, TOPK):
                    od2.link(STT(y, ring[0:n, 4 * i + c, 0:D], gate[0:n, i, c:c + 1], y, ALU.mult, ALU.add))
                od2.link(TT(y, y, g2row[0:n, i // 2, :], ALU.mult))
                od2.link(TT(y, y, x1tok[0:n, i, :], ALU.add), sem("res_ready"))
            dve.wait_ge(sem("fg_in"), 16)
            for i in range(3):
                n = P if i < 2 else TS
                dve.wait_ge(sem("frstd_ready"), i + 1)
                y = ring[0:n, 12 + i, 0:D]
                od2.did(STT(y, y, sumsq[0:n, i:i + 1], fgrow[0:n, :], ALU.mult, ALU.mult), sem("y_ready"))


_INS = ["x_prompt", "x_sample", "state_hgrn", "state_gla", "c_prompt", "c_sample", "norm1_g", "norm2_g", "w_ada", "b_ada",
        "w_in", "w_gk2", "b_gk2", "gn_hgrn", "gn_gla", "w_o", "router_w", "router_b", "w_up", "b_up", "w_down", "b_down",
        "final_norm_g"]
_OUTS = [("yp", (1, TP, D)), ("ys", (TS, 1, D)), ("hgp", (1, 1, 4, P, P)), ("glp", (1, 1, 4, 64, P)),
         ("hgs", (1, TS, 4, P, P)), ("gls", (1, TS, 4, 64, P))]


def kernel(**inputs):
    import numpy as np
    import concourse.bacc as bacc
    from concourse.bass_utils import run_bass_kernel_spmd

    nc = bacc.Bacc("TRN2", target_bir_lowering=False, num_devices=1)
    arrays, ins = {}, {}
    for name in _INS:
        x = np.ascontiguousarray(inputs[name])
        arrays[f"in_{name}"] = x
        ins[name] = nc.dram_tensor(f"in_{name}", x.shape, mybir.dt.from_np(x.dtype), kind="ExternalInput").ap()
    outs = {name: nc.dram_tensor(f"out_{name}", shape, F, kind="ExternalOutput").ap() for name, shape in _OUTS}
    build_step(nc, ins, outs)
    r = run_bass_kernel_spmd(nc, [arrays], core_ids=[0])
    return tuple(r.results[0][f"out_{name}"] for name, _ in _OUTS)
```
